# Optimizing a Trainium2 kernel written in Bass

```python
import jax, jax.numpy as jnp
from jax import lax
import numpy as np

D_MODEL = 1024
BATCH = 1
SEQ = 1024
DEPTH = 2

GRID_W = 64
CTX_LEN = 256
EPS = 1e-6

W_CONV = 1024
CONV_K = 3
N_HEADS_NA = 16
HEAD_DIM_NA = 64
W_NA = N_HEADS_NA * HEAD_DIM_NA
WIN_R = 8
WIN_C = 16
OFF_AB = 0
OFF_AC = W_CONV
OFF_AX = 2 * W_CONV
OFF_AG = 3 * W_CONV
OFF_Q = 4 * W_CONV
OFF_K = OFF_Q + W_NA
OFF_V = OFF_K + W_NA
OFF_BG = OFF_V + W_NA
E_IN = OFF_BG + W_NA
E_MIX = W_CONV + W_NA

W_RNN = 2048
N_BLK = 8
BLK = W_RNN // N_BLK
CONV_K_RNN = 4
LRU_C = 8.0
N_DIR = 2

N_EVEN = (DEPTH + 1) // 2
N_ODD = DEPTH // 2

kernel_name = "hybrid_conv_natten_rglru_diffusion_block"

def _rmsnorm(x, g):
    xf = x.astype(jnp.float32)
    y = xf * lax.rsqrt(jnp.mean(xf * xf, axis=-1, keepdims=True) + EPS)
    return (y * g.astype(jnp.float32)).astype(x.dtype)

def _dwconv(x, w, left):
    k = w.shape[0]
    return lax.conv_general_dilated(
        x, w[:, None, :].astype(x.dtype), window_strides=(1,),
        padding=[(left, k - 1 - left)], dimension_numbers=("NWC", "WIO", "NWC"),
        feature_group_count=x.shape[-1])

def _context_attention(q, k, v):
    bsz, L, H, dh = q.shape
    s = jnp.einsum("bqhd,bkhd->bhqk", q, k).astype(jnp.float32)
    p = jax.nn.softmax(s, axis=-1).astype(q.dtype)
    return jnp.einsum("bhqk,bkhd->bqhd", p, v).reshape(bsz, L, H * dh)

def _neighbourhood_attention(q, k, v, k_ctx, v_ctx, rpb):
    bsz, S, H, dh = q.shape
    rows = S // GRID_W
    kr = min(WIN_R, rows)
    n_win = kr * WIN_C
    qg = q.reshape(bsz, rows, GRID_W, H, dh)
    kg = k.reshape(bsz, rows, GRID_W, H, dh)
    vg = v.reshape(bsz, rows, GRID_W, H, dh)
    cols = np.arange(GRID_W)
    col_start = np.clip(cols - WIN_C // 2, 0, GRID_W - WIN_C)
    col_idx = col_start[:, None] + np.arange(WIN_C)[None, :]
    col_bias_idx = col_idx - cols[:, None] + (WIN_C - 1)

    def row_block(r):
        rs = jnp.clip(r - WIN_R // 2, 0, rows - kr)
        k_band = lax.dynamic_slice_in_dim(kg, rs, kr, axis=1)
        v_band = lax.dynamic_slice_in_dim(vg, rs, kr, axis=1)
        k_win = k_band[:, :, col_idx]
        v_win = v_band[:, :, col_idx]
        q_r = lax.dynamic_index_in_dim(qg, r, axis=1, keepdims=False)
        row_bias_idx = rs + jnp.arange(kr) - r + (WIN_R - 1)
        bias = rpb[:, row_bias_idx[None, :, None], col_bias_idx[:, None, :]]
        s_win = jnp.einsum("bqhd,brqjhd->bhqrj", q_r, k_win).astype(jnp.float32) + bias.astype(jnp.float32)
        s_ctx = jnp.einsum("bqhd,bkhd->bhqk", q_r, k_ctx).astype(jnp.float32)
        s = jnp.concatenate([s_win.reshape(bsz, H, GRID_W, n_win), s_ctx], axis=-1)
        p = jax.nn.softmax(s, axis=-1).astype(q.dtype)
        p_win = p[..., :n_win].reshape(bsz, H, GRID_W, kr, WIN_C)
        return (jnp.einsum("bhqrj,brqjhd->bqhd", p_win, v_win)
                + jnp.einsum("bhqk,bkhd->bqhd", p[..., n_win:], v_ctx))

    out = lax.map(row_block, jnp.arange(rows))
    return jnp.moveaxis(out, 0, 1).reshape(bsz, S, H * dh)

def _even_mixer(u_lat, u_ctx, w_in, w_conv, rpb, w_out, need_ctx):
    bsz, S, _ = u_lat.shape
    Lc = u_ctx.shape[1]
    scale = HEAD_DIM_NA ** -0.5
    z = u_lat @ w_in
    y_a = z[..., OFF_AB:OFF_AC] * _dwconv(z[..., OFF_AC:OFF_AX] * z[..., OFF_AX:OFF_AG], w_conv, CONV_K // 2)
    y_a = y_a * jax.nn.silu(z[..., OFF_AG:OFF_Q])
    base = 0 if need_ctx else OFF_K
    zc = u_ctx @ (w_in if need_ctx else w_in[:, OFF_K:OFF_BG])
    k_c = zc[..., OFF_K - base:OFF_V - base].reshape(bsz, Lc, N_HEADS_NA, HEAD_DIM_NA)
    v_c = zc[..., OFF_V - base:OFF_BG - base].reshape(bsz, Lc, N_HEADS_NA, HEAD_DIM_NA)
    q = z[..., OFF_Q:OFF_K].reshape(bsz, S, N_HEADS_NA, HEAD_DIM_NA) * scale
    k = z[..., OFF_K:OFF_V].reshape(bsz, S, N_HEADS_NA, HEAD_DIM_NA)
    v = z[..., OFF_V:OFF_BG].reshape(bsz, S, N_HEADS_NA, HEAD_DIM_NA)
    y_b = _neighbourhood_attention(q, k, v, k_c, v_c, rpb) * jax.nn.silu(z[..., OFF_BG:E_IN])
    y_lat = jnp.concatenate([y_a, y_b], axis=-1) @ w_out
    if not need_ctx:
        return y_lat, None
    yc_a = zc[..., OFF_AB:OFF_AC] * _dwconv(zc[..., OFF_AC:OFF_AX] * zc[..., OFF_AX:OFF_AG], w_conv, CONV_K // 2)
    yc_a = yc_a * jax.nn.silu(zc[..., OFF_AG:OFF_Q])
    q_c = zc[..., OFF_Q:OFF_K].reshape(bsz, Lc, N_HEADS_NA, HEAD_DIM_NA) * scale
    yc_b = _context_attention(q_c, k_c, v_c) * jax.nn.silu(zc[..., OFF_BG:E_IN])
    y_ctx = jnp.concatenate([yc_a, yc_b], axis=-1) @ w_out
    return y_lat, y_ctx

def _rglru_coeffs(xs, w_ra, b_ra, w_ri, b_ri, lam):
    bsz, L, _ = xs.shape
    xb = xs.reshape(bsz, L, N_BLK, BLK)

    def blockdiag(w, bias):
        return (jnp.einsum("blnk,dnkm->dblnm", xb, w).reshape(N_DIR, bsz, L, W_RNN)
                + bias[:, None, None, :]).astype(jnp.float32)

    r = jax.nn.sigmoid(blockdiag(w_ra, b_ra))
    i = jax.nn.sigmoid(blockdiag(w_ri, b_ri))
    log_a = LRU_C * r * jax.nn.log_sigmoid(lam.astype(jnp.float32))[:, None, None, :]
    a = jnp.exp(log_a)
    b = jnp.sqrt(-jnp.expm1(2.0 * log_a)) * i * xs.astype(jnp.float32)[None]
    return a, b

def _bidir_scan(a, b, h0):
    def scan_order(z):
        return jnp.moveaxis(jnp.stack([z[0], jnp.flip(z[1], axis=1)]), 2, 0)

    def step(h, ab):
        h = ab[0] * h + ab[1]
        return h, h

    h_T, hs = lax.scan(step, h0, (scan_order(a), scan_order(b)))
    y = hs[:, 0] + jnp.flip(hs[:, 1], axis=0)
    return h_T, jnp.moveaxis(y, 0, 1)

def _odd_mixer(u_lat, u_ctx, w_in, conv_w, conv_b, w_ra, b_ra, w_ri, b_ri, lam, w_out, need_ctx):
    bsz = u_lat.shape[0]
    left = (CONV_K_RNN - 1) // 2
    z = u_lat @ w_in
    zc = u_ctx @ (w_in if need_ctx else w_in[:, :W_RNN])
    x_l = _dwconv(z[..., :W_RNN], conv_w, left) + conv_b
    x_c = _dwconv(zc[..., :W_RNN], conv_w, left) + conv_b
    a_c, b_c = _rglru_coeffs(x_c, w_ra, b_ra, w_ri, b_ri, lam)
    h_ctx_T, y_c = _bidir_scan(a_c, b_c, jnp.zeros((N_DIR, bsz, W_RNN), jnp.float32))
    a_l, b_l = _rglru_coeffs(x_l, w_ra, b_ra, w_ri, b_ri, lam)
    _, y_l = _bidir_scan(a_l, b_l, h_ctx_T)
    y_lat = (y_l.astype(u_lat.dtype) * jax.nn.silu(z[..., W_RNN:])) @ w_out
    if not need_ctx:
        return y_lat, None
    y_ctx = (y_c.astype(u_ctx.dtype) * jax.nn.silu(zc[..., W_RNN:])) @ w_out
    return y_lat, y_ctx

def setup_inputs(seed: int = 0) -> dict:
    key = jax.random.key(seed)
    ks = jax.random.split(key, 24)
    f32 = jnp.float32

    def nrm(k, shape, s):
        return jax.random.normal(k, shape, f32) * s

    u = jax.random.uniform(ks[20], (N_ODD, N_DIR, W_RNN), f32, 0.9, 0.999)
    p = u ** (1.0 / LRU_C)
    lru_lam = jnp.log(p) - jnp.log1p(-p)
    return {
        "x": nrm(ks[0], (BATCH, SEQ, D_MODEL), 1.0),
        "c": nrm(ks[1], (BATCH, D_MODEL), 1.0),
        "ctx": nrm(ks[2], (BATCH, CTX_LEN, D_MODEL), 1.0),
        "c_ctx": nrm(ks[3], (D_MODEL,), 1.0),
        "norm_g": 1.0 + nrm(ks[4], (DEPTH, D_MODEL), 0.05),
        "w_ada": nrm(ks[5], (DEPTH, D_MODEL, 3 * D_MODEL), 0.5 * D_MODEL ** -0.5),
        "b_ada": nrm(ks[6], (DEPTH, 3 * D_MODEL), 0.02),
        "w_in_e": nrm(ks[7], (N_EVEN, D_MODEL, E_IN), D_MODEL ** -0.5),
        "conv_a": nrm(ks[8], (N_EVEN, CONV_K, W_CONV), CONV_K ** -0.5),
        "rpb": nrm(ks[9], (N_EVEN, N_HEADS_NA, 2 * WIN_R - 1, 2 * WIN_C - 1), 0.05),
        "w_out_e": nrm(ks[10], (N_EVEN, E_MIX, D_MODEL), E_MIX ** -0.5),
        "w_in_o": nrm(ks[11], (N_ODD, D_MODEL, 2 * W_RNN), D_MODEL ** -0.5),
        "conv_c": nrm(ks[12], (N_ODD, CONV_K_RNN, W_RNN), CONV_K_RNN ** -0.5),
        "conv_c_b": nrm(ks[13], (N_ODD, W_RNN), 0.02),
        "w_ra": nrm(ks[14], (N_ODD, N_DIR, N_BLK, BLK, BLK), BLK ** -0.5),
        "b_ra": nrm(ks[15], (N_ODD, N_DIR, W_RNN), 0.02),
        "w_ri": nrm(ks[16], (N_ODD, N_DIR, N_BLK, BLK, BLK), BLK ** -0.5),
        "b_ri": nrm(ks[17], (N_ODD, N_DIR, W_RNN), 0.02),
        "lru_lam": lru_lam,
        "w_out_o": nrm(ks[18], (N_ODD, W_RNN, D_MODEL), W_RNN ** -0.5),
        "final_g": 1.0 + nrm(ks[19], (D_MODEL,), 0.05),
    }

def reference(x, c, ctx, c_ctx, norm_g, w_ada, b_ada, w_in_e, conv_a, rpb, w_out_e,
              w_in_o, conv_c, conv_c_b, w_ra, b_ra, w_ri, b_ri, lru_lam, w_out_o, final_g):
    D = D_MODEL
    s_c = jax.nn.silu(c)
    s_cc = jax.nn.silu(c_ctx)
    h_lat, h_ctx = x, ctx
    for layer in range(DEPTH):
        need_ctx = layer < DEPTH - 1
        mod = s_c @ w_ada[layer] + b_ada[layer]
        shift, scale, gate = mod[:, None, :D], mod[:, None, D:2 * D], mod[:, None, 2 * D:]
        mod_c = s_cc @ w_ada[layer] + b_ada[layer]
        u_lat = _rmsnorm(h_lat, norm_g[layer]) * (1.0 + scale) + shift
        u_ctx = _rmsnorm(h_ctx, norm_g[layer]) * (1.0 + mod_c[D:2 * D]) + mod_c[:D]
        i = layer // 2
        if layer % 2 == 0:
            y_lat, y_ctx = _even_mixer(u_lat, u_ctx, w_in_e[i], conv_a[i], rpb[i], w_out_e[i], need_ctx)
        else:
            y_lat, y_ctx = _odd_mixer(u_lat, u_ctx, w_in_o[i], conv_c[i], conv_c_b[i], w_ra[i], b_ra[i],
                                      w_ri[i], b_ri[i], lru_lam[i], w_out_o[i], need_ctx)
        h_lat = h_lat + gate * y_lat
        if need_ctx:
            h_ctx = h_ctx + mod_c[2 * D:] * y_ctx
    return _rmsnorm(h_lat, final_g)


_drawn_inputs = setup_inputs


def setup_inputs(seed=0):
    import zlib

    import numpy as np

    out = dict(_drawn_inputs(seed))
    spreads = {}
    factors = {'rpb': 64.0, 'b_ra': 42.24, 'b_ri': 8.0}
    for name, (base, spread) in spreads.items():
        noise = np.random.default_rng([zlib.crc32(name.encode()), seed]).standard_normal(out[name].shape)
        drawn = base * np.exp(spread * noise) if base else spread * noise
        out[name] = __import__('jax').numpy.asarray(drawn.astype(out[name].dtype))
    for name, factor in factors.items():
        out[name] = (out[name] * factor).astype(out[name].dtype)
    return out
```

```python
from contextlib import ExitStack

import numpy as np

import concourse.bass as bass
from concourse import mybir

F32 = mybir.dt.float32
F32R = mybir.dt.float32r
ALU = mybir.AluOpType
ACT = mybir.ActivationFunctionType
AX_X = mybir.AxisListType.X

P = 128
D = 1024
LAT, CTX = 1024, 256
TOK = LAT + CTX
KC = D // P
NT = TOK // P
NLT = LAT // P
EPS = 1e-6
GRID_W, WIN_R, WIN_C = 64, 8, 16
ROWS = LAT // GRID_W
HD = 64
PAIRS = 8
E_IN = 8192
NE_CHUNKS = E_IN // P
YC = 16
BLOCKS = 8
NEG = -1.0e30

GROUPS = [(0, 428), (428, 854), (854, 1280)]
NG = len(GROUPS)

START = [min(max(2 * t - WIN_R // 2, 0), ROWS - WIN_R) for t in range(NLT)]
END = [min(max(2 * t + 1 - WIN_R // 2, 0), ROWS - WIN_R) + WIN_R for t in range(NLT)]
TROW = [START[t] - 2 * t + WIN_R - 1 for t in range(NLT)]
TROWS = 2 * WIN_R
MID = WIN_R - 1 - WIN_R // 2
MIDROWS = WIN_R + 1


def pads(t):
    return t + 1 if t < LAT else t + 3


def split_at_ctx(a, b):
    if a < LAT < b:
        return [(a, LAT), (LAT, b)]
    return [(a, b)]


class Map:

    BASE = 16512
    TOP = 229344

    def __init__(self, nc, start):
        self.nc, self.at = nc, start

    def __call__(self, name, shape, dt=F32):
        t = self.nc.alloc_sbuf_tensor_at(name, shape, dt, offset=self.BASE + self.at)
        self.at += (int(np.prod(shape[1:])) * 4 + 31) // 32 * 32
        assert self.BASE + self.at <= self.TOP, (name, self.at)
        return t


class Link:

    def __init__(self, eng, s, i=0, per=0, base=0):
        self.eng, self.s, self.i, self.per, self.base, self.n = eng, s, i, per, base, 0

    def __call__(self, ins):
        self.n += 1
        ins.then_inc(self.s, 1)
        self.eng.wait_ge(self.s, self.i * self.per + (self.base + self.n))


U_BYTES = 2 * KC * TOK * 4
CONST_BYTES = 2560
PHASE = U_BYTES + CONST_BYTES


def build_program(nc, a, out, upto=5):
    ctx = ExitStack()
    with ctx:
        def sem(name):
            return ctx.enter_context(nc.semaphore(name))

        cm = Map(nc, U_BYTES)
        k = dict(
            ident=cm("ident", [P, P]),
            mod0=cm("mod0", [P, 16, 2]),
            modx=cm("modx", [P, 32, 2]),
            bada=cm("bada", [P, 48, 2]),
            normg=cm("normg", [P, 2, KC, 2]),
            gs=cm("gs", [P, 2, 2, KC, 2]),
            eps=cm("eps", [P, 1]),
        )
        ps = ctx.enter_context(nc.psum_tensor("ps", [P, 8, 512], F32))
        dram = dict(
            y0=nc.dram_tensor("y0_scratch", (YC, P, TOK), F32, kind="Internal").ap(),
            h0=nc.dram_tensor("h0_scratch", (NT, P, 512), F32, kind="Internal").ap(),
            h1=nc.dram_tensor("h1_scratch", (NLT, P, D), F32, kind="Internal").ap(),
            y1=nc.dram_tensor("y1_scratch", (YC, P, LAT), F32, kind="Internal").ap(),
            h2=nc.dram_tensor("h2_scratch", (NLT, P, 512), F32, kind="Internal").ap(),
        )
        uhi = nc.alloc_sbuf_tensor_at("u_hi", [P, KC, TOK], F32R, offset=Map.BASE)
        ulo = nc.alloc_sbuf_tensor_at("u_lo", [P, KC, TOK], F32R, offset=Map.BASE + U_BYTES // 2)
        env = dict(nc=nc, a=a, out=out, sem=sem, k=k, ps=ps, dram=dram, uhi=uhi, ulo=ulo, ctx=ctx)
        mod_and_norm(**env)
        if upto >= 2:
            even_layer(**env)
        if upto >= 3:
            out_projection(layer=0, **env)
        if upto >= 4:
            odd_layer(**env)
        if upto >= 5:
            out_projection(layer=1, **env)


def mod_and_norm(nc, a, out, sem, k, ps, dram, uhi, ulo, ctx):
    m = Map(nc, PHASE)
    x = m("x_tiles", [P, NT, D])
    ada = m("ada_pieces", [P, 4, 2, KC // 2 * 512])
    row = m("mod_rows", [2, 4, 512])
    small = m("c_cols", [P, KC, 2])
    th = m("c_tanh", [P, KC, 2])
    ss = m("sum_squares", [P, NT])
    rms = m("rms", [P, NT])
    rinv = m("rms_inverse", [P, NT])
    k["silu_c"] = nc.alloc_sbuf_tensor_at("silu_c", [P, KC, 2], F32, offset=Map.BASE + U_BYTES + CONST_BYTES - 64)
    xt = nc.alloc_sbuf_tensor_at("x_norm_t", [P, KC, TOK], F32, offset=Map.BASE + U_BYTES // 2)

    x_loaded = [sem(f"x_loaded{i}") for i in range(NT // 2)]
    ada_loaded = [sem(f"ada0_loaded{i}") for i in range(4)]
    c_loaded = sem("c_loaded")
    eps_set, squared, root_done, rinv_done, x_scaled = (
        sem("eps_set"), sem("squared"), sem("root_done"), sem("rinv_done"), sem("x_scaled"))
    c_tanh, silu_done, ada_mm, mod_done = sem("c_tanh_done"), sem("silu_done"), sem("ada0_mm"), sem("mod0_done")
    turned, out_act, out_dve = sem("x_turned"), sem("xt_by_act"), sem("xt_by_dve")
    modulated, hi_done, lo_done = sem("modulated"), sem("u_hi_done"), sem("u_lo_done")
    pool_lo, row_copied, mod_turned = sem("u_lo_by_pool"), sem("mod_row_copied"), sem("mod_turned")

    def bank(v):
        return ps[:, v % 4, :]

    with nc.Block() as block:
        @block.sync
        def _(sp):
            for name in ("ident", "bada", "normg"):
                sp.dma_start(k[name][:], a[name]).then_inc(c_loaded, 16)
            sp.dma_start(small[:], a["c_cols"]).then_inc(c_loaded, 16)
            xin = a["x"].rearrange("b (t p) d -> p (b t) d", p=P)
            cin = a["ctx"].rearrange("b (t p) d -> p (b t) d", p=P)
            for t in range(0, NLT, 2):
                sp.dma_start(x[:, t:t + 2, :], xin[:, t:t + 2, :]).then_inc(x_loaded[t // 2], 16)
            sp.dma_start(x[:, NLT:NT, :], cin).then_inc(x_loaded[NLT // 2], 16)
            for j in range(4):
                sp.dma_start(ada[:, j], a["w_ada"][j].rearrange("h p n -> p h n")).then_inc(ada_loaded[j], 16)

        @block.scalar
        def _(act):
            act.wait_ge(c_loaded, 64)
            nc.scalar.activation(th[:], small[:], ACT.Tanh, scale=0.5).then_inc(c_tanh, 1)
            for t in range(NT):
                act.wait_ge(x_loaded[t // 2], 16)
                act.wait_ge(squared, t)
                nc.scalar.activation(ps[:, 6:8, :].rearrange("p a b -> p (a b)"), x[:, t, :], ACT.Square,
                                     accum_out=ss[:, t:t + 1]).then_inc(squared, 1)
            act.wait_ge(squared, NT)
            act.wait_ge(eps_set, 1)
            nc.scalar.activation(rms[:], ss[:], ACT.Sqrt, scale=1.0 / D, bias=k["eps"][:, 0:1]).then_inc(root_done, 1)
            for v in range(0, 2 * NT, 2):
                act.wait_ge(turned, v + 1)
                t = v // 2
                nc.scalar.activation(xt[:, 0:4, t * P:(t + 1) * P], bank(v).rearrange("p (c n) -> p c n", c=4),
                                     ACT.Copy).then_inc(out_act, 1)
            for j in range(4):
                act.wait_ge(ada_mm, j + 1)
                nc.scalar.activation(row[:, j, :], ps[0:2, 4 + j % 2, :], ACT.Copy).then_inc(row_copied, 1)
            for c in range(KC):
                act.wait_ge(modulated, 2 * (c + 1))
                nc.scalar.activation(uhi[:, c, :], xt[:, c, :], ACT.Copy).then_inc(hi_done, 1)

        @block.vector
        def _(dve):
            nc.vector.memset(k["eps"][:], EPS).then_inc(eps_set, 1)
            dve.wait_ge(c_tanh, 1)
            nc.vector.scalar_tensor_tensor(out=th[:], in0=th[:], scalar=1.0, in1=small[:],
                                           op0=ALU.add, op1=ALU.mult).then_inc(silu_done, 1)
            dve.wait_ge(silu_done, 1)
            nc.vector.tensor_scalar(k["silu_c"][:], th[:], 0.5, None, ALU.mult).then_inc(silu_done, 1)
            dve.wait_ge(root_done, 1)
            link = Link(dve, rinv_done)
            link(nc.vector.reciprocal(rms[:], rms[:]))
            link(nc.vector.tensor_scalar(ss[:], ss[:], 1.0 / D, EPS, ALU.mult, ALU.add))
            for _ in range(2):
                link(nc.vector.tensor_tensor(ss[:], ss[:], rms[:], ALU.mult))
            link(nc.vector.tensor_scalar(ss[:], ss[:], -0.5, 1.5, ALU.mult, ALU.add))
            link(nc.vector.tensor_tensor(rinv[:], ss[:], rms[:], ALU.mult))
            for t in range(NT):
                nc.vector.tensor_scalar(x[:, t, :], x[:, t, :], rinv[:, t:t + 1], None,
                                        ALU.mult).then_inc(x_scaled, 1)
            for v in range(1, 2 * NT, 2):
                dve.wait_ge(turned, v + 1)
                t = v // 2
                nc.vector.tensor_copy(xt[:, 4:8, t * P:(t + 1) * P],
                                      bank(v).rearrange("p (c n) -> p c n", c=4)).then_inc(out_dve, 1)
            dve.wait_ge(mod_turned, 1)
            nc.vector.tensor_tensor(k["mod0"][:], ps[:, 6, 0:32].rearrange("p (c s) -> p c s", s=2),
                                    k["bada"][:, 0:16, :], ALU.add).then_inc(mod_done, 1)
            dve.wait_ge(mod_done, 1)
            nc.vector.scalar_tensor_tensor(out=k["gs"][:, 0, 0], in0=k["mod0"][:, 8:16, :], scalar=1.0,
                                           in1=k["normg"][:, 0], op0=ALU.add, op1=ALU.mult).then_inc(mod_done, 1)
            nc.vector.tensor_copy(k["gs"][:, 0, 1], k["mod0"][:, 0:8, :]).then_inc(mod_done, 1)
            dve.wait_ge(mod_done, 3)
            dve.wait_ge(out_act, NT)
            dve.wait_ge(out_dve, NT)
            for c in range(KC + 1):
                if c < KC:
                    for s, (f, g) in enumerate(((0, LAT), (LAT, TOK))):
                        nc.vector.tensor_scalar(xt[:, c, f:g], xt[:, c, f:g], k["gs"][:, 0, 0, c, s:s + 1],
                                                k["gs"][:, 0, 1, c, s:s + 1], ALU.mult, ALU.add).then_inc(modulated, 1)
                if c > 0 and (c - 1) % 4 != 3:
                    dve.wait_ge(hi_done, c)
                    nc.vector.tensor_tensor(ulo[:, c - 1, :], xt[:, c - 1, :], uhi[:, c - 1, :].bitcast(F32),
                                            ALU.subtract).then_inc(lo_done, 1)

        @block.gpsimd
        def _(pool):
            for c in (3, 7):
                pool.wait_ge(hi_done, c + 1)
                nc.gpsimd.tensor_tensor(ulo[:, c, :], xt[:, c, :], uhi[:, c, :].bitcast(F32),
                                        ALU.subtract).then_inc(pool_lo, 1)

        @block.tensor
        def _(pe):
            pe.wait_ge(c_loaded, 64)
            for v in range(2 * NT):
                t = v // 2
                if v % 2 == 0:
                    pe.wait_ge(x_scaled, t + 1)
                if v >= 4:
                    pe.wait_ge(out_dve if v % 2 else out_act, (v - 4) // 2 + 1)
                for q in range(4):
                    c = 4 * (v % 2) + q
                    last = nc.tensor.transpose(bank(v)[:, q * P:(q + 1) * P], x[:, t, c * P:(c + 1) * P], k["ident"][:])
                last.then_inc(turned, 1)
            pe.wait_ge(silu_done, 2)
            for j in range(5):
                if j < 4:
                    pe.wait_ge(ada_loaded[j], 16)
                    if j >= 2:
                        pe.wait_ge(row_copied, j - 1)
                    for c in range(KC):
                        last = nc.tensor.matmul(ps[0:2, 4 + j % 2, :], k["silu_c"][:, c, :],
                                                ada[:, j, c // 4, (c % 4) * 512:(c % 4 + 1) * 512],
                                                start=(c == 0), stop=(c == KC - 1))
                    last.then_inc(ada_mm, 1)
                if j > 0:
                    pe.wait_ge(row_copied, j)
                    for q in range(4):
                        at = 2 * (4 * (j - 1) + q)
                        last = nc.tensor.transpose(ps[:, 6, at:at + 2], row[:, j - 1, q * P:(q + 1) * P],
                                                   k["ident"][0:2, 0:2])
            last.then_inc(mod_turned, 1)


BG, CC, CX, CB, CG, CQ, CK, CV = range(8)
STEPS = 2 * NT
ORDER = [(j, g) for j in range(CC, CV + 1) for g in range(NG)]


def even_layer(nc, a, out, sem, k, ps, dram, uhi, ulo, ctx):
    m = Map(nc, PHASE)
    stage = m("w_stage", [P, 2, KC * P])
    whi, wlo = m("w_hi", [P, 2, KC * P], F32R), m("w_lo", [P, 2, KC * P], F32R)
    ada = m("ada_piece", [P, KC // 2 * 512])
    row = m("mod_row", [2, 512])
    conv_start = m.at
    cbuf, pbuf, acc = m("conv_c", [P, TOK]), m("conv_in", [P, TOK + 4]), m("conv_out", [P, TOK + 4])
    m.at = conv_start
    raw_q, raw_k = m("raw_q", [P, TOK]), m("raw_k", [P, TOK + 4])
    raw_v = m("raw_v", [P, TOK + 4])
    th = m("gate_tanh", [P, TOK])
    qst = m("q_stack", [P, 2, TOK], F32R)
    kst = m("k_stack", [P, 2, TOK], F32R)
    klo = m("k_lo", [P, TOK], F32R)
    vst = m("v_stack", [P, NT, 2, P], F32R)
    gate = m("branch_gate", [P, TOK])
    yb = m("y_attn", [P, TOK])
    table = m("bias_table", [P, 2, TROWS * GRID_W])
    mid = m("bias_mid", [P, MIDROWS * GRID_W])
    colmask, rowmask = m("colmask", [P, GRID_W]), m("rowmask", [P, MIDROWS])
    convw = m("conv_w", [P, 24])
    prob = m("probs", [P, 2, 832])
    pt = m("probs_t", [P, 7, 2 * P], F32R)
    low, t2 = m("pv_low", [P, 2 * P]), m("pv_out", [P, P])
    mx, negmax, sums = m("row_max", [P, 2, 2]), m("neg_max", [P, 2]), m("row_sums", [P, 2, 2])
    tot, rcp = m("row_total", [P, 2]), m("row_rcp", [P, 2])

    s_const = sem("even_consts")
    w_loaded = [sem("w_loaded0"), sem("w_loaded1")]
    w_hi, w_lo, proj = sem("w_hi_done"), sem("w_lo_done"), sem("proj_done")
    bank_free = [sem("proj_bank_read0"), sem("proj_bank_read1")]
    st_hi, st_lo, v_turned = sem("stack_hi_done"), sem("stack_lo_done"), sem("v_turned")
    scored, neg_ready, exped, normed = sem("scores_done"), sem("neg_max_ready"), sem("exp_done"), sem("probs_normed")
    turned, pt_hi, pt_lo = sem("probs_turned"), sem("probs_t_hi"), sem("probs_t_lo")
    pv_done, low_done, pv_used, yb_done = sem("pv_done"), sem("pv_low_copied"), sem("pv_read"), sem("y_attn_done")
    gate_t = sem("gate_tanh_done")
    ya_done, ya_stored, yb_stored = sem("y_conv_done"), sem("y_conv_stored"), sem("y_attn_stored")
    t_loaded = [sem("table_loaded_a"), sem("table_loaded_b")]
    t_ready = [sem("table_ready_a"), sem("table_ready_b")]
    mid_ready, pool_link = sem("table_mid_ready"), sem("pool_link")
    a_loaded, a_mm, row_done, mod_turned, mod_copied = (
        sem("ada_loaded"), sem("ada_mm"), sem("mod_row_done"), sem("modx_turned"), sem("modx_copied"))
    dve_link = sem("even_dve_link")
    DVE_PER = 2 * (NLT * 4 + (NT - NLT) * 3) + 4

    def chunk(i, j):
        return i * 8 + (3 + j)

    def unit(i, j, g):
        return i * 24 + (9 + 3 * j + g)

    def half(i, j, g):
        return i * 12 + (9 + 3 * j + g) // 2

    def bank(j, g):
        return (9 + 3 * j + g) % 2

    def step_unit(s, last):
        order = [o for o in ORDER if o[0] < CQ] if last else ORDER
        return order[s:s + 1] if s < STEPS - 1 else order[s:]

    def tile_of(s):
        return s // NT, s % NT

    def window(t):
        return GRID_W * (END[t] - START[t]) if t < NLT else 0

    def blocks(t):
        found = [(576 + P * b, P, NLT + b) for b in range(CTX // P)]
        w = window(t)
        for b in range((w + P - 1) // P):
            found.append((P * b, min(P, w - P * b), START[t] * GRID_W // P + b))
        return found

    def run(eng, prologue, body):
        prologue()
        with eng.Fori(0, PAIRS - 1) as i:
            body(i, False)
        body(PAIRS - 1, True)

    def load_table(eng, h, i, head):
        rows = a["bias_rows"]
        for r in range(2):
            heads = bass.AP(tensor=rows.tensor, offset=r * P,
                            ap=[[(TROWS + 1) * P, 2 * PAIRS], [1, GRID_W], [P, TROWS], [1, GRID_W]])
            src = heads[head]
            eng.dma_start(table[GRID_W * r:GRID_W * (r + 1), h, :].rearrange("p (e c) -> p e c", e=TROWS),
                          src).then_inc(t_loaded[h], 16)

    with nc.Block() as block:
        @block.sync
        def _(sp):
            def load(g, slot, n):
                sp.dma_start(stage[:, slot, :], a["w_even"][g]).then_inc(w_loaded[slot], 16)

            def prologue():
                for dst, name in ((colmask, "colmask"), (rowmask, "rowmask"), (convw, "conv_a")):
                    sp.dma_start(dst[:], a[name]).then_inc(s_const, 16)
                load(0, 0, 0)
                load(1, 1, 0)
                sp.wait_ge(w_lo, 1)
                load(2, 0, 1)

            def body(i, last):
                for j in range(CQ if last else CV + 1):
                    sp.wait_ge(w_lo, i * 8 + (2 + j))
                    load(chunk(i, j), (3 + j) % 2, 0)
                    if j in (CC, CG):
                        half_k = 0 if j == CC else 1
                        sp.wait_ge(a_mm, 2 * i + half_k)
                        sp.dma_start(ada[:], a["w_ada"][4 + i, half_k]).then_inc(a_loaded, 16)

            run(sp, prologue, body)

        @block.gpsimd
        def _(pool):
            def split_lo(g, slot):
                pool.wait_ge(w_hi, g + 1)
                nc.gpsimd.tensor_tensor(wlo[:, slot, :], stage[:, slot, :], whi[:, slot, :].bitcast(F32),
                                        ALU.subtract).then_inc(w_lo, 1)

            def build_table(h, i, n):
                pool.wait_ge(t_loaded[h], n * 32)
                t = table[:, h, :].rearrange("p (e c) -> p e c", e=TROWS)
                nc.gpsimd.tensor_tensor(t, t, colmask[:].unsqueeze(1).to_broadcast([P, TROWS, GRID_W]),
                                        ALU.add).then_inc(t_ready[h], 1)

            def build_mid(h, n):
                pool.wait_ge(t_ready[h], n)
                t = table[:, h, :].rearrange("p (e c) -> p e c", e=TROWS)[:, MID:MID + MIDROWS, :]
                nc.gpsimd.tensor_tensor(mid[:].rearrange("p (e c) -> p e c", e=MIDROWS), t,
                                        rowmask[:].unsqueeze(2).to_broadcast([P, MIDROWS, GRID_W]),
                                        ALU.add).then_inc(mid_ready, 1)

            def prologue():
                pool.wait_ge(s_const, 48)
                split_lo(0, 0)
                build_table(0, 0, 1)
                build_mid(0, 1)
                split_lo(1, 1)
                split_lo(2, 0)

            def body(i, last):
                for j in range(CQ if last else CV + 1):
                    split_lo(chunk(i, j), (3 + j) % 2)
                    if j == CC:
                        build_table(1, i, i + 1)
                    if j == CG:
                        pool.wait_ge(neg_ready, i * STEPS + 6)
                        build_mid(1, i + 1)
                    if j == CK:
                        build_table(0, i, i + 2)
                    if j == CV:
                        pool.wait_ge(neg_ready, i * STEPS + 16)
                        build_mid(0, i + 2)

            run(pool, prologue, body)

        @block.scalar
        def _(act):
            def split_hi(i, c):
                act.wait_ge(w_loaded[c % 2], i * 64 + 16 * (c // 2 + 1))
                if c >= 2:
                    act.wait_ge(proj, i * 24 + 3 * (c - 1))
                nc.scalar.activation(whi[:, c % 2, :], stage[:, c % 2, :], ACT.Copy).then_inc(w_hi, 1)

            def copy_unit(i, j, g, dst, scale=1.0):
                f, t = GROUPS[g]
                act.wait_ge(proj, unit(i, j, g) + 1)
                nc.scalar.activation(dst[:, f:t], ps[:, bank(j, g), 0:t - f], ACT.Copy,
                                     scale=scale).then_inc(bank_free[bank(j, g)], 1)

            def tanh_unit(i, j, g):
                f, t = GROUPS[g]
                act.wait_ge(proj, unit(i, j, g) + 1)
                if j == BG:
                    act.wait_ge(ya_done, i)
                else:
                    act.wait_ge(bank_free[bank(BG, g)], half(i, BG, g) + 1)
                nc.scalar.activation(th[:, f:t], ps[:, bank(j, g), 0:t - f], ACT.Tanh,
                                     scale=0.5).then_inc(gate_t, 1)

            def qkv_unit(i, j, g):
                if j == CQ and g == 0:
                    act.wait_ge(ya_done, i + 1)
                if j == CV and g == 0:
                    act.wait_ge(ya_stored, 32 * (i + 1))
                copy_unit(i, j, g, {CQ: raw_q, CK: raw_k, CV: raw_v}[j], 0.125 if j == CQ else 1.0)

            def project(i, j, g, last):
                if j == CC:
                    if g == 0:
                        act.wait_ge(st_lo, i * 6 + 6)
                        act.wait_ge(v_turned, 2 * i + 2)
                    copy_unit(i, j, g, cbuf)
                elif j in (BG, CG):
                    tanh_unit(i, j, g)
                elif j >= CQ:
                    qkv_unit(i, j, g)
                if g == NG - 1 and not (last and j + 2 > CG):
                    split_hi(i, 3 + j + 2)

            def exp(i, s):
                h, t = tile_of(s)
                w, b = window(t), s % 2
                act.wait_ge(neg_ready, i * STEPS + (s + 1))
                if w:
                    nc.scalar.activation(prob[:, b, 0:w], prob[:, b, 0:w], ACT.Exp, bias=negmax[:, b:b + 1],
                                         accum_out=sums[:, b, 0:1])
                nc.scalar.activation(prob[:, b, 576:832], ps[:, 3, 64:320], ACT.Exp, bias=negmax[:, b:b + 1],
                                     accum_out=sums[:, b, 1:2]).then_inc(exped, 1)

            def turn_hi(i, s):
                h, t = tile_of(s)
                bl = blocks(t)
                full = sum(n == P for _, n, _ in bl)
                act.wait_ge(turned, i * STEPS + (s + 1))
                ins = nc.scalar.activation(pt[:, 0:full, 0:P],
                                           ps[:, 4:6, :].rearrange("p a (b n) -> p (a b) n", n=P)[:, 0:full, :], ACT.Copy)
                if full < len(bl):
                    ins = nc.scalar.activation(pt[0:64, full, 0:P],
                                               ps[0:64, 4 + full // 4, (full % 4) * P:(full % 4 + 1) * P], ACT.Copy)
                ins.then_inc(pt_hi, 1)

            def copy_low(i, s):
                h, t = tile_of(s)
                act.wait_ge(pv_done, i * STEPS + (s + 1))
                nc.scalar.activation(low[HD * h:HD * (h + 1), :], ps[64:128, 6, 0:2 * P], ACT.Copy).then_inc(low_done, 1)

            def stack(i, h):
                r = slice(HD * h, HD * (h + 1))
                o = slice(HD * (1 - h), HD * (2 - h))
                nc.scalar.activation(qst[r, h, :], raw_q[r, ::-1], ACT.Copy).then_inc(st_hi, 1)
                nc.scalar.activation(kst[r, h, :], raw_k[r, 0:TOK], ACT.Copy).then_inc(st_hi, 1)
                nc.scalar.activation(kst[o, h, :], raw_k[r, 0:TOK], ACT.Copy).then_inc(st_hi, 1)

            def prologue():
                load_table(act, 0, 0, 0)
                load_table(act, 1, 0, 1)
                split_hi(0, 0)
                split_hi(0, 1)
                for j in (CQ, CK, CV):
                    for g in range(NG):
                        copy_unit(-1, j, g, {CQ: raw_q, CK: raw_k, CV: raw_v}[j], 0.125 if j == CQ else 1.0)
                    split_hi(0, j - CQ + 2)

            def body(i, last):
                act.wait_ge(bank_free[bank(BG, 1)], half(i, BG, 1))
                stack(i, 0)
                project(i, BG, 0, last)
                act.wait_ge(v_turned, 2 * i + 1)
                nc.scalar.activation(vst[:, 0:8, :, 0:HD],
                                     ps[:, 4:6, :].rearrange("p a (b h n) -> p (a b) h n", h=2, n=HD), ACT.Copy).then_inc(st_hi, 1)
                act.wait_ge(v_turned, 2 * i + 2)
                nc.scalar.activation(vst[:, 8:10, :, 0:HD],
                                     ps[:, 7, 0:2 * P].rearrange("p (b h n) -> p b h n", h=2, n=HD), ACT.Copy).then_inc(st_hi, 1)
                exp(i, 0)
                stack(i, 1)
                project(i, BG, 1, last)
                project(i, BG, 2, last)
                for s in range(STEPS):
                    turn_hi(i, s)
                    if s + 1 < STEPS:
                        exp(i, s + 1)
                    for j, g in step_unit(s, last):
                        project(i, j, g, last)
                    copy_low(i, s)
                    if s == 11:
                        act.wait_ge(a_mm, 2 * i + 2)
                        nc.scalar.activation(row[:], ps[0:2, 7, :], ACT.Copy).then_inc(row_done, 1)
                    if s == 13:
                        act.wait_ge(ya_done, i + 1)
                        store_conv(act, i)
                    if s == 9 and not last:
                        act.wait_ge(neg_ready, i * STEPS + 8)
                        load_table(act, 0, i, 2 * i + 2)
                    if s == 18 and not last:
                        act.wait_ge(neg_ready, i * STEPS + 18)
                        load_table(act, 1, i, 2 * i + 3)
                act.wait_ge(yb_done, i * STEPS + STEPS)
                act.dma_start(dram["y0"][8 + i], yb[:]).then_inc(yb_stored, 16)

            def store_conv(eng, i):
                eng.dma_start(dram["y0"][i][:, 0:LAT], acc[:, 1:LAT + 1]).then_inc(ya_stored, 16)
                eng.dma_start(dram["y0"][i][:, LAT:TOK], acc[:, LAT + 3:TOK + 3]).then_inc(ya_stored, 16)

            run(act, prologue, body)
            act.wait_ge(ya_stored, 32 * PAIRS)
            act.wait_ge(yb_stored, 16 * PAIRS)

        @block.vector
        def _(dve):
            def read(j, g, f=None, t=None):
                a0, b0 = GROUPS[g]
                f, t = a0 if f is None else f, b0 if t is None else t
                return ps[:, bank(j, g), f - a0:t - a0]

            def project(i, j, g, link):
                f0, t0 = GROUPS[g]
                free = bank_free[bank(j, g)]
                if j in (CC, CQ, CK, CV):
                    return
                if j in (BG, CG):
                    dve.wait_ge(gate_t, i * 6 + (g + 1 + (3 if j == CG else 0)))
                if j == BG:
                    nc.vector.scalar_tensor_tensor(out=gate[:, f0:t0], in0=th[:, f0:t0], scalar=1.0,
                                                   in1=read(j, g), op0=ALU.add, op1=ALU.mult).then_inc(free, 1)
                if j == CG:
                    nc.vector.scalar_tensor_tensor(out=th[:, f0:t0], in0=th[:, f0:t0], scalar=1.0,
                                                   in1=read(j, g), op0=ALU.add, op1=ALU.mult).then_inc(free, 1)
                    dve.wait_ge(free, half(i, j, g) + 1)
                    for f, t in split_at_ctx(f0, t0):
                        q = slice(pads(f), pads(f) + t - f)
                        ins = nc.vector.scalar_tensor_tensor(out=acc[:, q], in0=th[:, f:t], scalar=0.5,
                                                             in1=acc[:, q], op0=ALU.mult, op1=ALU.mult)
                    if g == NG - 1:
                        ins.then_inc(ya_done, 1)
                if j == CX:
                    dve.wait_ge(proj, unit(i, j, g) + 1)
                    dve.wait_ge(bank_free[bank(CC, g)], half(i, CC, g) + 1)
                    if g == 0:
                        for q in (slice(0, 1), slice(LAT + 1, LAT + 3), slice(TOK + 3, TOK + 4)):
                            ins = nc.vector.memset(pbuf[:, q], 0.0)
                        link(ins)
                    for f, t in split_at_ctx(f0, t0):
                        ins = nc.vector.tensor_tensor(pbuf[:, pads(f):pads(f) + t - f], read(j, g, f, t),
                                                      cbuf[:, f:t], ALU.mult)
                    ins.then_inc(free, 1)
                    if g == NG - 1:
                        dve.wait_ge(free, half(i, j, g) + 1)
                        w = [convw[:, bass.ds(i * 3 + tap, 1)] for tap in range(3)]
                        n = TOK + 2
                        link(nc.vector.tensor_scalar(acc[:, 1:n + 1], pbuf[:, 0:n], w[0], None, ALU.mult))
                        for tap in (1, 2):
                            link(nc.vector.scalar_tensor_tensor(out=acc[:, 1:n + 1], in0=pbuf[:, tap:n + tap], scalar=w[tap],
                                                                in1=acc[:, 1:n + 1], op0=ALU.mult, op1=ALU.add))
                if j == CB:
                    dve.wait_ge(proj, unit(i, j, g) + 1)
                    for f, t in split_at_ctx(f0, t0):
                        q = slice(pads(f), pads(f) + t - f)
                        ins = nc.vector.tensor_tensor(acc[:, q], read(j, g, f, t), acc[:, q], ALU.mult)
                    ins.then_inc(free, 1)
                    dve.wait_ge(free, half(i, j, g) + 1)

            def row_max(i, s, link):
                h, t = tile_of(s)
                w, b = window(t), s % 2
                dve.wait_ge(scored, i * STEPS + (s + 1))
                if w:
                    if t == 0:
                        dve.wait_ge(t_ready[h], i + 1)
                    if t == 2:
                        dve.wait_ge(mid_ready, 2 * i + (1 + h))
                red = nc.vector.tensor_reduce(mx[:, b, 1:2], ps[:, 3, 64:320], AX_X, ALU.max)
                if not w:
                    link(red)
                if w:
                    bias = mid[:] if w == MIDROWS * GRID_W else table[:, h, TROW[t] * GRID_W:TROW[t] * GRID_W + w]
                    link(nc.vector.tensor_tensor_reduce(prob[:, b, 0:w], ps[:, 2:4, :].rearrange("p a n -> p (a n)")[:, 0:w],
                                                        bias, 1.0, NEG, ALU.add, ALU.max, mx[:, b, 0:1]))
                if w:
                    nc.vector.tensor_scalar(negmax[:, b:b + 1], mx[:, b, 0:1], mx[:, b, 1:2], -1.0,
                                            ALU.max, ALU.mult).then_inc(neg_ready, 1)
                else:
                    nc.vector.tensor_scalar(negmax[:, b:b + 1], mx[:, b, 1:2], -1.0, None,
                                            ALU.mult).then_inc(neg_ready, 1)

            def normalise(i, s, link):
                h, t = tile_of(s)
                w, b = window(t), s % 2
                dve.wait_ge(exped, i * STEPS + (s + 1))
                if w:
                    link(nc.vector.tensor_tensor(tot[:, b:b + 1], sums[:, b, 0:1], sums[:, b, 1:2], ALU.add))
                link(nc.vector.reciprocal(rcp[:, b:b + 1], tot[:, b:b + 1] if w else sums[:, b, 1:2]))
                for q in ([slice(0, 832)] if w == 576 else [slice(0, 512), slice(576, 832)] if w else [slice(576, 832)]):
                    ins = nc.vector.tensor_scalar(prob[:, b, q], prob[:, b, q], rcp[:, b:b + 1], None, ALU.mult)
                ins.then_inc(normed, 1)

            def turn_lo(i, s):
                h, t = tile_of(s)
                bl = blocks(t)
                full = sum(n == P for _, n, _ in bl)
                dve.wait_ge(pt_hi, i * STEPS + (s + 1))
                ins = nc.vector.tensor_tensor(pt[:, 0:full, P:2 * P],
                                              ps[:, 4:6, :].rearrange("p a (b n) -> p (a b) n", n=P)[:, 0:full, :],
                                              pt[:, 0:full, 0:P].bitcast(F32), ALU.subtract)
                if full < len(bl):
                    ins = nc.vector.tensor_tensor(pt[0:64, full, P:2 * P],
                                                  ps[0:64, 4 + full // 4, (full % 4) * P:(full % 4 + 1) * P],
                                                  pt[0:64, full, 0:P].bitcast(F32), ALU.subtract)
                ins.then_inc(pt_lo, 1)

            def output(i, s, link):
                h, t = tile_of(s)
                r = slice(HD * h, HD * (h + 1))
                dve.wait_ge(low_done, i * STEPS + (s + 1))
                if s == 0:
                    dve.wait_ge(yb_stored, 16 * i)
                nc.vector.tensor_tensor(low[r, :], ps[0:64, 6, 0:2 * P], low[r, :], ALU.add).then_inc(pv_used, 1)
                dve.wait_ge(pv_used, i * STEPS + (s + 1))
                link(nc.vector.tensor_tensor(t2[r, :], low[r, 0:P], low[r, P:2 * P], ALU.add))
                q = slice((t + 1) * P - 1, t * P - 1 if t else None, -1)
                nc.vector.scalar_tensor_tensor(out=yb[r, q], in0=t2[r, :], scalar=0.5, in1=gate[r, q],
                                               op0=ALU.mult, op1=ALU.mult).then_inc(yb_done, 1)

            def stack(i, h, first):
                r = slice(HD * h, HD * (h + 1))
                o = slice(HD * (1 - h), HD * (2 - h))
                dve.wait_ge(st_hi, i * 8 + (first + 1))
                nc.vector.tensor_tensor(qst[o, h, :], raw_q[r, ::-1], qst[r, h, :].bitcast(F32),
                                        ALU.subtract).then_inc(st_lo, 1)
                dve.wait_ge(st_hi, i * 8 + (first + 3))
                nc.vector.tensor_tensor(klo[r, :], raw_k[r, 0:TOK], kst[r, h, :].bitcast(F32),
                                        ALU.subtract).then_inc(st_lo, 1)

            def body(i, last):
                link = Link(dve, dve_link, i, DVE_PER)
                stack(i, 0, 0)
                project(i, BG, 0, link)
                dve.wait_ge(st_hi, i * 8 + 4)
                nc.vector.tensor_tensor(vst[:, 0:8, :, HD:P], ps[:, 4:6, :].rearrange("p a (b h n) -> p (a b) h n", h=2, n=HD),
                                        vst[:, 0:8, :, 0:HD].bitcast(F32), ALU.subtract).then_inc(st_lo, 1)
                dve.wait_ge(st_hi, i * 8 + 5)
                nc.vector.tensor_tensor(vst[:, 8:10, :, HD:P], ps[:, 7, 0:2 * P].rearrange("p (b h n) -> p b h n", h=2, n=HD),
                                        vst[:, 8:10, :, 0:HD].bitcast(F32), ALU.subtract).then_inc(st_lo, 1)
                row_max(i, 0, link)
                normalise(i, 0, link)
                stack(i, 1, 5)
                project(i, BG, 1, link)
                project(i, BG, 2, link)
                for s in range(STEPS):
                    if s + 1 < STEPS:
                        row_max(i, s + 1, link)
                    turn_lo(i, s)
                    if s + 1 < STEPS:
                        normalise(i, s + 1, link)
                    for j, g in step_unit(s, last):
                        project(i, j, g, link)
                    output(i, s, link)
                    if s == 15:
                        dve.wait_ge(mod_turned, i + 1)
                        nc.vector.tensor_tensor(k["modx"][:, bass.ds(i * 4, 4), :], ps[:, 7, 0:8].rearrange("p (c s) -> p c s", s=2),
                                                k["bada"][:, bass.ds(i * 4 + 16, 4), :], ALU.add).then_inc(mod_copied, 1)
                assert link.n == DVE_PER, link.n

            def prologue():
                dve.wait_ge(s_const, 48)

            run(dve, prologue, body)

        @block.tensor
        def _(pe):
            def project(i, j, g):
                f, t = GROUPS[g]
                slot = (3 + j) % 2
                if g == 0:
                    pe.wait_ge(w_lo, chunk(i, j) + 1)
                if not (isinstance(i, int) and half(i, j, g) < 1):
                    pe.wait_ge(bank_free[bank(j, g)], half(i, j, g))
                parts = ((whi, uhi), (whi, ulo), (wlo, uhi))
                for c in range(KC):
                    for n, (w, x) in enumerate(parts):
                        last = nc.tensor.matmul(ps[:, bank(j, g), 0:t - f], w[:, slot, c * P:(c + 1) * P], x[:, c, f:t],
                                                start=(c == 0 and n == 0), stop=(c == KC - 1 and n == 2))
                last.then_inc(proj, 1)

            def scores(i, s):
                h, t = tile_of(s)
                w = window(t)
                if s in (0, NT):
                    pe.wait_ge(st_hi, i * 8 + (8 if h else 3))
                    pe.wait_ge(st_lo, i * 6 + (6 if h else 2))
                pe.wait_ge(exped, i * STEPS + s)
                hi = slice(HD * h, HD * (h + 1))
                q = slice(TOK - (t + 1) * P, TOK - t * P)
                k0 = GRID_W * START[t] if w else 0
                parts = [(2, 0, k0, min(w, 512)), (3, 0, k0 + 512, w - 512), (3, 64, LAT, CTX)]
                for bk, col, tok, n in parts:
                    if n > 0:
                        nc.tensor.matmul(ps[:, bk, col:col + n], qst[:, h, q], kst[:, h, tok:tok + n], start=True, stop=False)
                        last = nc.tensor.matmul(ps[:, bk, col:col + n], qst[hi, h, q], klo[hi, tok:tok + n],
                                                start=False, stop=True)
                last.then_inc(scored, 1)

            def turn(i, s):
                h, t = tile_of(s)
                pe.wait_ge(normed, i * STEPS + (s + 1))
                pe.wait_ge(pt_lo, i * STEPS + s)
                for b, (col, n, _) in enumerate(blocks(t)):
                    last = nc.tensor.transpose(ps[0:n, 4 + b // 4, (b % 4) * P:(b % 4 + 1) * P],
                                               prob[:, s % 2, col:col + n], k["ident"][:])
                last.then_inc(turned, 1)

            def weigh(i, s):
                h, t = tile_of(s)
                if s == 0:
                    pe.wait_ge(st_lo, i * 6 + 4)
                pe.wait_ge(pt_lo, i * STEPS + (s + 1))
                pe.wait_ge(pv_used, i * STEPS + s)
                bl = blocks(t)
                for b, (_, n, vt) in enumerate(bl):
                    last = nc.tensor.matmul(ps[:, 6, 0:2 * P], vst[0:n, vt, h, :], pt[0:n, b, :],
                                            start=(b == 0), stop=(b == len(bl) - 1))
                last.then_inc(pv_done, 1)

            def prologue():
                for j in (CQ, CK, CV):
                    for g in range(NG):
                        project(-1, j, g)

            def body(i, last):
                pe.wait_ge(bank_free[bank(BG, 1)], half(i, BG, 1))
                pe.wait_ge(pt_lo, i * STEPS)
                for t in range(NLT):
                    ins = nc.tensor.transpose(ps[:, 4 + t // 4, (t % 4) * P:(t % 4 + 1) * P], raw_v[:, t * P:(t + 1) * P],
                                              k["ident"][:])
                ins.then_inc(v_turned, 1)
                pe.wait_ge(mod_copied, i)
                for t in range(NLT, NT):
                    ins = nc.tensor.transpose(ps[:, 7, (t - NLT) * P:(t - NLT + 1) * P], raw_v[:, t * P:(t + 1) * P],
                                              k["ident"][:])
                ins.then_inc(v_turned, 1)
                project(i, BG, 0)
                scores(i, 0)
                project(i, BG, 1)
                project(i, BG, 2)
                for s in range(STEPS):
                    if s + 1 < STEPS:
                        scores(i, s + 1)
                    if s == 0:
                        pe.wait_ge(st_lo, i * 6 + 4)
                    turn(i, s)
                    if s == 14:
                        pe.wait_ge(row_done, i + 1)
                        if last:
                            pe.wait_ge(exped, i * STEPS + s)
                    for j, g in step_unit(s, last):
                        project(i, j, g)
                    weigh(i, s)
                    if s in (4, 10):
                        kh = 0 if s == 4 else 1
                        pe.wait_ge(a_loaded, i * 32 + 16 * (kh + 1))
                        for c in range(KC // 2):
                            ins = nc.tensor.matmul(ps[0:2, 7, :], k["silu_c"][:, KC // 2 * kh + c, :],
                                                   ada[:, c * 512:(c + 1) * 512], start=(kh == 0 and c == 0),
                                                   stop=(kh == 1 and c == KC // 2 - 1))
                        ins.then_inc(a_mm, 1)
                    if s == 14:
                        for q in range(4):
                            ins = nc.tensor.transpose(ps[:, 7, 2 * q:2 * q + 2], row[:, q * P:(q + 1) * P], k["ident"][0:2, 0:2])
                        ins.then_inc(mod_turned, 1)

            run(pe, prologue, body)


def out_projection(layer, nc, a, out, sem, k, ps, dram, uhi, ulo, ctx):
    n = NT if layer == 0 else NLT
    WBYTES = YC * 512 * 4

    def tag(name):
        return f"{name}_{layer}"

    def s_(name):
        return sem(tag(name))

    w0 = [nc.alloc_sbuf_tensor_at(tag("wout0_" + part), [P, YC, 512], F32R, offset=Map.BASE + r * WBYTES)
          for r, part in enumerate(("hi", "lo"))]
    m = Map(nc, PHASE)
    w1 = [m(tag("wout1_" + part), [P, YC, 512], F32R) for part in ("hi", "lo")]
    w = [w0, w1]
    raw = [nc.alloc_sbuf_tensor_at(tag(f"wout{q}_raw"), [P, YC, 512], F32, offset=at + WBYTES)
           for q, at in enumerate((Map.BASE, Map.BASE + PHASE))]
    yraw = m(tag("y_tile"), [P, 2, YC // 2, P])
    yhi, ylo = m(tag("y_hi"), [P, 2, YC, P], F32R), m(tag("y_lo"), [P, 2, YC, P], F32R)
    ut, xn = m(tag("u_tile"), [P, KC, P]), m(tag("xn_tile"), [P, D])
    diag = ut[:].rearrange("p (s c) n -> p s (c n)", s=2)
    fg = xn
    grow = m(tag("gate_row"), [P, 2, 512])
    h = m(tag("h_tile"), [P, 2, 512])
    xh = m(tag("x_half"), [P, 2, 512])
    ones = m(tag("ones"), [P, P])
    ss, rms, rinv, var, nw = (m(tag(x), [P, 1]) for x in ("ss", "rms", "rinv", "var", "newton"))
    y, hs = dram["y0" if layer == 0 else "y1"], dram["h0" if layer == 0 else "h2"]
    gcol = 0 if layer == 0 else 24

    w_loaded = [s_(f"wout_loaded{q}") for q in range(4)]
    w_hi, w_lo = s_("wout_hi"), s_("wout_lo")
    y_loaded, y_hi, y_lo = [s_("y_loaded0"), s_("y_loaded1")], s_("y_hi_done"), s_("y_lo_done")
    x_loaded = [s_("x_half_loaded0"), s_("x_half_loaded1")]
    mm_done, h_done = s_("out_mm_done"), s_("h_done")
    diag_done, row_mm, row_done, const_done = s_("diag_done"), s_("gate_row_mm"), s_("gate_row_done"), s_("out_consts")
    h_stored = [s_("h_half_stored0"), s_("h_half_stored1")]
    ha_loaded, h1_stored = s_("h_half_loaded"), s_("h_stored")
    squared, rooted, rinv_done = s_("squared"), s_("rooted"), s_("rinv_done")
    links = [s_("out_link0"), s_("out_link1")]
    if layer == 0:
        xn_done, turned, applied = s_("xn_done"), s_("h_turned"), s_("u_applied")
        u_hi_done, u_lo_done = s_("u_hi_done"), s_("u_lo_done")
    else:
        fg_loaded, normed = s_("final_g_loaded"), s_("row_normed")
    HALF_ITS = n // 2
    LOOPS = HALF_ITS - 2

    def run(part_a, part_b, pass_, index):
        part_a(pass_, 0, 0, None)

        def body(i, at):
            last = at == HALF_ITS - 1
            for d in (1, 2):
                if not (last and d == 2):
                    part_a(pass_, 2 * i + d, d % 2, i)
                part_b(pass_, 2 * i + (d - 1), (d - 1) % 2, i)

        with index(0, LOOPS) as i:
            body(i, 0)
        for i in range(LOOPS, HALF_ITS):
            body(i, i)

    def stream(t):
        return 1 if isinstance(t, int) and t >= NLT else 0

    def x_tile(t, f, g):
        if layer == 1:
            return dram["h1"][t][:, f:g]
        if stream(t):
            return a["ctx"][0, (t - NLT) * P:(t - NLT + 1) * P, f:g]
        return a["x"].rearrange("b (t p) d -> (b t) p d", p=P)[t][:, f:g]

    with nc.Block() as block:
        @block.sync
        def _(sp):
            def load_w(pass_, q):
                if pass_:
                    sp.wait_ge(w_hi, 2 * q + 2)
                sp.dma_start(raw[pass_][:, 4 * q:4 * q + 4, :].rearrange("p (r k) n -> p r (k n)", r=2),
                             a[f"w_out{layer}"][pass_, 2 * q:2 * q + 2].rearrange("r p n -> p r n")).then_inc(w_loaded[q], 16)

            def load_y(q, t):
                for half in range(2):
                    if not (isinstance(q, int) and q == 0):
                        sp.wait_ge(y_lo, 2 * q + (half - 1))
                    sp.dma_start(yraw[:, half], y.rearrange("(a c) p (t n) -> t a p c n", n=P, a=2)[t, half]
                                 ).then_inc(y_loaded[half], 16)

            def load_x(pass_, t, b):
                sp.wait_ge(h_done, pass_ * n + t + 1)
                sp.dma_start(xh[:, b, :], x_tile(t, 512 * pass_, 512 * pass_ + 512)).then_inc(x_loaded[b], 16)

            def load_tile(pass_, t, b):
                load_y(pass_ * n + t, t)
                load_x(pass_, t, b)

            load_y(0, 0)
            load_w(0, 0)
            load_w(0, 1)
            load_x(0, 0, 0)
            load_w(0, 2)
            load_w(0, 3)
            load_tile(0, 1, 1)
            for q in range(4):
                load_w(1, q)
            with sp.Fori(1, 4) as i:
                for b in range(2):
                    load_tile(0, 2 * i + b, b)
            if n == NT:
                for b in range(2):
                    load_tile(0, 8 + b, b)
            with sp.Fori(0, 4) as i:
                for b in range(2):
                    load_tile(1, 2 * i + b, b)
            if n == NT:
                for b in range(2):
                    load_tile(1, 8 + b, b)

        @block.gpsimd
        def _(pool):
            nc.gpsimd.memset(ones[:], 1.0).then_inc(const_done, 1)
            if layer == 1:
                pool.dma_start(fg[:], a["final_g"].partition_broadcast(P)).then_inc(fg_loaded, 16)
            pool.wait_ge(w_lo, 8)
            for r in range(8):
                pool.wait_ge(w_hi, 8 + r + 1)
                c = slice(2 * r, 2 * r + 2)
                nc.gpsimd.tensor_tensor(w[1][1][:, c, :], raw[1][:, c, :], w[1][0][:, c, :].bitcast(F32), ALU.subtract).then_inc(w_lo, 1)

        @block.scalar
        def _(act):
            def split_w(p):
                r = p % 8
                act.wait_ge(w_loaded[r // 2], 16 * (p // 8 + 1))
                nc.scalar.activation(w[p // 8][0][:, 2 * r:2 * r + 2, :], raw[p // 8][:, 2 * r:2 * r + 2, :],
                                     ACT.Copy).then_inc(w_hi, 1)

            def split_y(q, b):
                act.wait_ge(mm_done, q + 1)
                for half in range(2):
                    act.wait_ge(y_loaded[half], q * 16 + 16)
                    nc.scalar.activation(yhi[:, b, half * 8:half * 8 + 8], yraw[:, half], ACT.Copy).then_inc(y_hi, 1)

            def copy_rows(pass_):
                act.wait_ge(row_mm, pass_ + 1)
                if pass_:
                    act.wait_ge(h_done, n + 2)
                nc.scalar.activation(grow[:], ps[:, 6:8, :], ACT.Copy).then_inc(row_done, 1)

            def part_a(pass_, t, b, i):
                q = pass_ * n + t
                if not (pass_ == 1 and isinstance(t, int) and t >= n - 2):
                    split_y(q + 2, b)
                if pass_ == 0:
                    act.wait_ge(h_done, q + 3)
                    act.dma_start(hs[t], h[:, b, :]).then_inc(h_stored[b], 16)
                    return
                act.wait_ge(h_done, q + 3)
                act.wait_ge(ha_loaded, t * 16 + 16)
                if layer == 0 and not stream(t):
                    act.dma_start(dram["h1"][t], h[:].rearrange("p a n -> p (a n)")).then_inc(h1_stored, 16)
                act.wait_ge(squared, t)
                nc.scalar.activation(ps[:, 4:6, :], h[:], ACT.Square, accum_out=ss[:]).then_inc(squared, 1)
                act.wait_ge(squared, t + 1)
                nc.scalar.activation(rms[:], ss[:], ACT.Sqrt, scale=1.0 / D, bias=k["eps"][:, 0:1]).then_inc(rooted, 1)
                if layer == 0:
                    act.wait_ge(rinv_done, t + 1)
                    act.wait_ge(turned, t)
                    nc.scalar.activation(xn[:], h[:].rearrange("p a n -> p (a n)"), ACT.Copy,
                                         scale=rinv[:, 0:1]).then_inc(xn_done, 1)
                    if isinstance(t, int) and t == n - 1:
                        return
                    act.wait_ge(xn_done, t + 1)
                    act.wait_ge(h1_stored, 16 * (min(t + 1, NLT) if isinstance(t, int) else t + 1))
                else:
                    act.wait_ge(normed, t + 1)
                    act.dma_start(out[0].rearrange("(t p) d -> t p d", p=P)[t],
                                  h[:].rearrange("p a n -> p (a n)")).then_inc(h1_stored, 16)
                    if isinstance(t, int) and t == n - 1:
                        return
                    act.wait_ge(h1_stored, (t + 1) * 16)
                act.dma_start(h[:, 0, :], hs[t + 1]).then_inc(ha_loaded, 16)

            def part_b(pass_, t, b, i):
                if pass_ == 1 and layer == 0:
                    act.wait_ge(applied, t + 1)
                    nc.scalar.activation(uhi[:, :, bass.ds(t * P, P)], ut[:], ACT.Copy).then_inc(u_hi_done, 1)

            split_y(0, 0)
            for p in range(8):
                split_w(p)
            copy_rows(0)
            split_y(1, 1)

            for i in range(HALF_ITS):
                for b in range(2):
                    part_a(0, 2 * i + b, b, i)
                    if i < 2:
                        for p in range(2):
                            split_w(8 + 4 * i + 2 * b + p)
            for b in range(2):
                act.wait_ge(h_stored[b], 16 * HALF_ITS)
            copy_rows(1)
            act.dma_start(h[:, 0, :], hs[0]).then_inc(ha_loaded, 16)
            run(part_a, part_b, 1, act.Fori)
            act.wait_ge(h1_stored, 16 * NLT)

        @block.vector
        def _(dve):
            dve.sem_inc(h_done, 2)

            def split_y(q, b):
                for half in range(2):
                    c = slice(half * 8, half * 8 + 8)
                    dve.wait_ge(y_hi, 2 * q + (half + 1))
                    nc.vector.tensor_tensor(ylo[:, b, c], yraw[:, half], yhi[:, b, c].bitcast(F32),
                                            ALU.subtract).then_inc(y_lo, 1)

            def split_w(r):
                c = slice(2 * r, 2 * r + 2)
                dve.wait_ge(w_hi, r + 1)
                nc.vector.tensor_tensor(w[0][1][:, c, :], raw[0][:, c, :], w[0][0][:, c, :].bitcast(F32), ALU.subtract).then_inc(w_lo, 1)

            def diagonals(pass_):
                for s in range(2):
                    for c in range(4):
                        ins = nc.vector.tensor_scalar(diag[:, s, c * P:(c + 1) * P], k["ident"][:],
                                                      k["modx"][:, gcol + 4 * pass_ + c, s:s + 1], None, ALU.mult)
                ins.then_inc(diag_done, 1)

            def link_for(pass_, i):
                per = (1, 5)[pass_] * 2
                return Link(dve, links[pass_], 0 if i is None else i, per, 0 if i is None else per // 2)

            state = {}

            def part_a(pass_, t, b, i):
                q = pass_ * n + t
                if b == 1 or i is None:
                    state["link"] = link_for(pass_, i)
                link = state["link"]
                s = stream(t)
                dve.wait_ge(x_loaded[b], pass_ * (16 * HALF_ITS) + (16 * (t // 2) + 16 if isinstance(t, int) else (i * 16 + (16 if b else 32))))
                dst = h[:, b, :] if pass_ == 0 else h[:, 1, :]
                if pass_ == 0:
                    dve.wait_ge(h_stored[b], 16 * (t // 2) if isinstance(t, int) else i * 16 + (0 if b else 16))
                elif layer == 0:
                    if not (isinstance(t, int) and t == 0):
                        dve.wait_ge(xn_done, t)
                        dve.wait_ge(h1_stored, 16 * (min(t, NLT) if isinstance(t, int) else t))
                else:
                    dve.wait_ge(h1_stored, t * 16)
                dve.wait_ge(row_done, pass_ + 1)
                dve.wait_ge(mm_done, q + 3)
                link(nc.vector.tensor_tensor(dst, ps[:, b, :], grow[:, s, :], ALU.mult))
                nc.vector.tensor_tensor(dst, dst, xh[:, b, :], ALU.add).then_inc(h_done, 1)
                if not (pass_ == 1 and isinstance(t, int) and t >= n - 2):
                    split_y(q + 2, b)
                if pass_ == 0:
                    return
                dve.wait_ge(rooted, t + 1)
                link(nc.vector.reciprocal(nw[:], rms[:]))
                link(nc.vector.tensor_scalar(var[:], ss[:], 1.0 / D, EPS, ALU.mult, ALU.add))
                link(nc.vector.scalar_tensor_tensor(out=var[:], in0=var[:], scalar=nw[:, 0:1], in1=nw[:],
                                                    op0=ALU.mult, op1=ALU.mult))
                link(nc.vector.tensor_scalar(var[:], var[:], -0.5, 1.5, ALU.mult, ALU.add))
                nc.vector.tensor_tensor(rinv[:], nw[:], var[:], ALU.mult).then_inc(rinv_done, 1)
                if layer == 1:
                    dve.wait_ge(rinv_done, t + 1)
                    dve.wait_ge(squared, t + 1)
                    dve.wait_ge(fg_loaded, 16)
                    nc.vector.scalar_tensor_tensor(out=h[:].rearrange("p a n -> p (a n)"),
                                                   in0=h[:].rearrange("p a n -> p (a n)"), scalar=rinv[:, 0:1],
                                                   in1=fg[:], op0=ALU.mult, op1=ALU.mult).then_inc(normed, 1)

            def part_b(pass_, t, b, i):
                if pass_ == 0 or layer == 1:
                    return
                dve.wait_ge(turned, t + 1)
                dve.wait_ge(u_lo_done, t)
                s = stream(t)
                for c in range(KC):
                    ins = nc.vector.tensor_scalar(ut[:, c, :], ps[:, 2 + c // 4, (c % 4) * P:(c % 4 + 1) * P],
                                                  k["gs"][:, 1, 0, c, s:s + 1], k["gs"][:, 1, 1, c, s:s + 1], ALU.mult, ALU.add)
                ins.then_inc(applied, 1)
                dve.wait_ge(u_hi_done, t + 1)
                nc.vector.tensor_tensor(ulo[:, :, bass.ds(t * P, P)], ut[:], uhi[:, :, bass.ds(t * P, P)].bitcast(F32),
                                        ALU.subtract).then_inc(u_lo_done, 1)

            if layer == 0:
                nc.vector.scalar_tensor_tensor(out=k["gs"][:, 1, 0], in0=k["modx"][:, 16:24, :], scalar=1.0,
                                               in1=k["normg"][:, 1], op0=ALU.add, op1=ALU.mult)
                nc.vector.tensor_copy(k["gs"][:, 1, 1], k["modx"][:, 8:16, :])
            diagonals(0)
            split_y(0, 0)
            for r in range(8):
                split_w(r)
            split_y(1, 1)
            dve.wait_ge(row_mm, 1)
            diagonals(1)
            run(part_a, part_b, 0, dve.Fori)
            for b in range(2):
                dve.wait_ge(h_stored[b], 16 * HALF_ITS)
            dve.wait_ge(row_mm, 2)
            run(part_a, part_b, 1, dve.Fori)

        @block.tensor
        def _(pe):
            pe.sem_inc(mm_done, 2)

            def gate_rows(pass_):
                pe.wait_ge(const_done, 1)
                pe.wait_ge(diag_done, pass_ + 1)
                for s in range(2):
                    ins = nc.tensor.matmul(ps[:, 6 + s, :], ones[:], diag[:, s, :], start=True, stop=True)
                ins.then_inc(row_mm, 1)

            def part_a(pass_, t, b, i):
                q = pass_ * n + t
                pe.wait_ge(h_done, q + 1)
                parts = ((yhi, 0), (yhi, 1), (ylo, 0))
                for c in range(YC):
                    if c % 8 == 0:
                        pe.wait_ge(y_lo, 2 * q + (c // 8 + 1))
                    if isinstance(t, int) and t == 0 and c % 2 == 0:
                        pe.wait_ge(w_lo, 8 * pass_ + c // 2 + 1)
                    for j, (yy, part) in enumerate(parts):
                        last = nc.tensor.matmul(ps[:, b, :], yy[:, b, c, :], w[pass_][part][:, c, :],
                                                start=(c == 0 and j == 0), stop=(c == YC - 1 and j == 2))
                last.then_inc(mm_done, 1)

            def part_b(pass_, t, b, i):
                if pass_ == 0 or layer == 1:
                    return
                pe.wait_ge(xn_done, t + 1)
                pe.wait_ge(applied, t)
                for c in range(KC):
                    last = nc.tensor.transpose(ps[:, 2 + c // 4, (c % 4) * P:(c % 4 + 1) * P], xn[:, c * P:(c + 1) * P],
                                               k["ident"][:])
                last.then_inc(turned, 1)

            for pass_ in range(2):
                gate_rows(pass_)
                run(part_a, part_b, pass_, pe.Fori)


CTX_COL = LAT + 3
QCOLS = 1284
QGROUPS = [(0, 428), (428, 856), (856, QCOLS)]
ZGROUPS = [(0, 512), (512, LAT)]
LOG_TERMS = 9


def odd_layer(nc, a, out, sem, k, ps, dram, uhi, ulo, ctx):
    m = Map(nc, PHASE)
    whi = m("o_w_hi", [P, 3, KC * P], F32R)
    wraw = nc.alloc_sbuf_tensor_at("o_w_raw", [P, 3, KC * P], F32, offset=Map.BASE + m.at)
    wlo = m("o_w_lo", [P, 3, KC * P], F32R)
    zr = m("conv_in4", [P, QCOLS + 4])
    xc = m("x_conv", [P, 2, QCOLS])
    xhi, xlo = m("x_hi", [P, 2, QCOLS], F32R), m("x_lo", [P, 2, QCOLS], F32R)
    R, E = m("lru_r", [P, QCOLS]), m("lru_root", [P, QCOLS])
    A, B = m("lru_a", [P, 2, QCOLS]), m("lru_b", [P, 2, QCOLS])
    H0, H1 = m("h_forward", [P, 2, QCOLS]), m("h_backward", [P, 2, QCOLS])
    sg = m("silu_gate", [P, 2, LAT])
    convw, convb = m("conv_w4", [P, 64]), m("conv_b4", [P, 16])
    lru, lam = m("lru_columns", [P, 5, 32]), m("lam", [P, 32])
    bri, bra, L, Lh, nLh = (lru[:, q, :] for q in range(5))
    own = m("lru_block_columns", [P, 5, 2, 2])
    e_, z_, z2, den, low = (m(x, [P, 32]) for x in ("log_e", "log_z", "log_z2", "log_den", "log_low"))

    s_const = sem("odd_consts")
    w_loaded = [sem(f"o_w_loaded{i}") for i in range(3)]
    w_hi, w_lo, proj = sem("o_w_hi_done"), sem("o_w_lo_done"), sem("o_proj_done")
    bank_free = [sem("o_bank_read0"), sem("o_bank_read1")]
    conv_done, xhi_done, xlo_done = sem("conv_done"), sem("x_hi_done"), sem("x_lo_done")
    gate_t, gate_mm, gate_read = sem("o_gate_tanh"), sem("lru_gate_mm"), sem("lru_gate_read")
    abs_done, e_done, consts_done = sem("lam_abs"), sem("lam_exp"), sem("lru_consts_done")
    a_done, th_done, v_done, root_done, b_done, scan_done = (
        sem("lru_a_done"), sem("lru_tanh_done"), sem("lru_v_done"), sem("lru_root_done"),
        sem("lru_b_done"), sem("lru_scan_done"))
    y_done = sem("o_y_done")
    y_stored = [sem("o_y_stored0"), sem("o_y_stored1")]
    own_done = sem("lru_block_columns_done")
    dve_link, dve_first = sem("odd_dve_link"), sem("odd_dve_first")
    DVE_PER = 2 * 3 + 4 * (1 + 1) + 2 * 1

    X1, Z0, GW0, Z1, GW1, X0 = range(6)
    OFF = {X1: 0, Z0: 3, Z1: 5, X0: 7}

    def chunk(n, j):
        return n * 6 + (1 + j)

    def unit(n, j, g):
        return n * 10 + (3 + OFF[j] + g)

    def half(n, j, g):
        return n * 5 + (3 + OFF[j] + g) // 2

    def bank(j, g):
        return (3 + OFF[j] + g) % 2

    def run(eng, prologue, body):
        prologue()
        with eng.Fori(0, BLOCKS - 1) as n:
            body(n, False)
        body(BLOCKS - 1, True)

    with nc.Block() as block:
        @block.sync
        def _(sp):
            def prologue():
                for dst, name in ((convw, "conv_c"), (convb, "conv_b"), (bra, "b_ra"), (bri, "b_ri"), (lam, "lam")):
                    sp.dma_start(dst if name in ("b_ra", "b_ri") else dst[:], a[name]).then_inc(s_const, 16)
                load(-1, X0)
                for j in range(3):
                    load(0, j)

            def load(n, j):
                if isinstance(n, int) and (n < 0 or (n == 0 and j < 2)):
                    pass
                elif j == X1:
                    sp.wait_ge(proj, unit(n, Z1, 1) + (1 - 10))
                elif j == Z0:
                    sp.wait_ge(gate_mm, n * 24)
                elif j == GW0:
                    sp.wait_ge(proj, unit(n, X0, 2) + (1 - 10))
                elif j == Z1:
                    sp.wait_ge(proj, unit(n, X1, 2) + 1)
                elif j == GW1:
                    sp.wait_ge(proj, unit(n, Z0, 1) + 1)
                else:
                    sp.wait_ge(gate_mm, n * 24 + 12)
                slot = (1 + j) % 3
                sp.dma_start(wraw[:, slot, :], a["w_odd"][chunk(n, j)]).then_inc(w_loaded[slot], 16)

            def store(n, mm):
                sp.wait_ge(y_done, 2 * n + (mm + 1))
                sp.dma_start(dram["y1"][2 * n + mm], H1[:, mm, 0:LAT]).then_inc(y_stored[mm], 16)

            def body(n, last):
                for j in (Z1, GW1) if last else (Z1, GW1, X0):
                    load(n, j)
                if not last:
                    load(n + 1, X1)
                store(n, 0)
                if not last:
                    load(n + 1, Z0)
                    load(n + 1, GW0)
                store(n, 1)

            run(sp, prologue, body)
            for mm in range(2):
                sp.wait_ge(y_stored[mm], 16 * BLOCKS)

        @block.gpsimd
        def _(pool):
            def split_lo(g, slot):
                pool.wait_ge(w_hi, g + 1)
                nc.gpsimd.tensor_tensor(wlo[:, slot, :], wraw[:, slot, :], whi[:, slot, :].bitcast(F32),
                                        ALU.subtract).then_inc(w_lo, 1)

            def body(n, last):
                for j in range(X0 if last else X0 + 1):
                    split_lo(chunk(n, j), (1 + j) % 3)

            run(pool, lambda: split_lo(0, 0), body)

        @block.scalar
        def _(act):
            def split_hi(n, j):
                c = 1 + j
                act.wait_ge(w_loaded[c % 3], n * 32 + 16 * (c // 3 + 1))
                nc.scalar.activation(whi[:, c % 3, :], wraw[:, c % 3, :], ACT.Copy).then_inc(w_hi, 1)

            def evacuate(n, j, g):
                if g == 0 and not (isinstance(n, int) and n < 0):
                    act.wait_ge(conv_done, 2 * n + (1 if j == X1 else 2))
                act.wait_ge(proj, unit(n, j, g) + 1)
                f, t = GROUPS[g]
                for c0, c1 in split_at_ctx(f, t):
                    at = c0 + 1 if c0 < LAT else c0 + 4
                    ins = nc.scalar.activation(zr[:, at:at + c1 - c0], ps[:, bank(j, g), c0 - f:c1 - f], ACT.Copy)
                ins.then_inc(bank_free[bank(j, g)], 1)

            def x_hi(n, mm):
                act.wait_ge(conv_done, 2 * n + (2 if mm else 3))
                if isinstance(n, int) and n < 0:
                    pass
                elif mm:
                    act.wait_ge(gate_mm, n * 24)
                else:
                    act.wait_ge(gate_mm, n * 24 + 24)
                nc.scalar.activation(xhi[:, mm, :], xc[:, mm, :], ACT.Copy).then_inc(xhi_done, 1)

            def tanh_z(n, j, g):
                mm = 0 if j == Z0 else 1
                f, t = ZGROUPS[g]
                act.wait_ge(y_done, 2 * n)
                act.wait_ge(proj, unit(n, j, g) + 1)
                nc.scalar.activation(sg[:, mm, f:t], ps[:, bank(j, g), :], ACT.Tanh, scale=0.5).then_inc(gate_t, 1)

            def col(q, p):
                return own[:, q, p // 2, p % 2:p % 2 + 1]

            def gate_units(n, p, mat):
                for g, (q0, q1) in enumerate(QGROUPS):
                    v = 6 * p + 3 * mat + g
                    act.wait_ge(gate_mm, n * 24 + (v + 1))
                    if mat == 0:
                        dst = B[:, p % 2, q0:q1]
                        if g == 0:
                            act.wait_ge(scan_done, n * 4 + max(p - 1, 0))
                    else:
                        dst = R[:, q0:q1]
                        if g == 0:
                            act.wait_ge(v_done, n * 4 + p)
                    ins = nc.scalar.activation(dst, ps[:, 2 + 3 * mat + g, 0:q1 - q0], ACT.Tanh, scale=0.5,
                                               bias=col(mat, p))
                    ins.then_inc(gate_read, 1)

            def decay(n, p):
                act.wait_ge(gate_read, n * 24 + (6 * p + 6) + 6)
                nc.scalar.activation(A[:, p % 2, :], R[:], ACT.Exp, scale=col(3, p), bias=col(3, p)).then_inc(a_done, 1)
                act.wait_ge(b_done, n * 4 + p)
                nc.scalar.activation(E[:], R[:], ACT.Exp, scale=col(2, p), bias=col(2, p))
                act.wait_ge(a_done, n * 4 + (p + 1))
                nc.scalar.activation(R[:], R[:], ACT.Tanh, scale=col(4, p), bias=col(4, p)).then_inc(th_done, 1)

            def root(n, p):
                act.wait_ge(v_done, n * 4 + (p + 1))
                nc.scalar.activation(E[:], E[:], ACT.Sqrt).then_inc(root_done, 1)

            def prologue():
                act.sem_inc(gate_read, 6)
                act.wait_ge(s_const, 80)
                split_hi(-1, X0)
                act.wait_ge(abs_done, 1)
                nc.scalar.activation(e_[:], e_[:], ACT.Exp, scale=-1.0).then_inc(e_done, 1)
                split_hi(0, X1)
                for g in range(NG):
                    evacuate(-1, X0, g)
                split_hi(0, Z0)
                x_hi(-1, 0)

            def body(n, last):
                for g in range(NG):
                    evacuate(n, X1, g)
                split_hi(n, GW0)
                tanh_z(n, Z0, 0)
                x_hi(n, 1)
                tanh_z(n, Z0, 1)
                split_hi(n, Z1)
                act.wait_ge(own_done, n + 1)
                gate_units(n, 0, 0)
                gate_units(n, 0, 1)
                decay(n, 0)
                tanh_z(n, Z1, 0)
                gate_units(n, 1, 0)
                root(n, 0)
                gate_units(n, 1, 1)
                split_hi(n, GW1)
                decay(n, 1)
                tanh_z(n, Z1, 1)
                if not last:
                    split_hi(n, X0)
                gate_units(n, 2, 0)
                root(n, 1)
                gate_units(n, 2, 1)
                decay(n, 2)
                if last:
                    gate_units(n, 3, 0)
                    root(n, 2)
                else:
                    evacuate(n, X0, 0)
                    root(n, 2)
                    evacuate(n, X0, 1)
                    split_hi(n + 1, X1)
                    evacuate(n, X0, 2)
                    gate_units(n, 3, 0)
                gate_units(n, 3, 1)
                decay(n, 3)
                if not last:
                    split_hi(n + 1, Z0)
                    x_hi(n, 0)
                root(n, 3)

            run(act, prologue, body)

        @block.vector
        def _(dve):
            def conv(n, mm, c, link):
                u = (n, X1, 2) if mm else (n, X0, 2)
                dve.wait_ge(bank_free[bank(u[1], 1)], half(n, u[1], 1) + 1)
                dve.wait_ge(bank_free[bank(u[1], 2)], half(n, u[1], 2) + 1)
                w = [convw[:, bass.ds(c * 4 + tap, 1)] for tap in range(4)]
                dst = xc[:, mm, :]
                link(nc.vector.tensor_scalar(dst, zr[:, 0:QCOLS], w[0], convb[:, bass.ds(c, 1)], ALU.mult, ALU.add))
                for tap in range(1, 4):
                    ins = nc.vector.scalar_tensor_tensor(out=dst, in0=zr[:, tap:QCOLS + tap], scalar=w[tap], in1=dst,
                                                         op0=ALU.mult, op1=ALU.add)
                    if tap < 3:
                        link(ins)
                ins.then_inc(conv_done, 1)

            def x_low(n, mm):
                dve.wait_ge(xhi_done, 2 * n + (2 if mm else 3))
                nc.vector.tensor_tensor(xlo[:, mm, :], xc[:, mm, :], xhi[:, mm, :].bitcast(F32),
                                        ALU.subtract).then_inc(xlo_done, 1)

            def silu_z(n, j, g):
                mm = 0 if j == Z0 else 1
                f, t = ZGROUPS[g]
                dve.wait_ge(gate_t, n * 4 + (2 * mm + g + 1))
                nc.vector.scalar_tensor_tensor(out=sg[:, mm, f:t], in0=sg[:, mm, f:t], scalar=1.0,
                                               in1=ps[:, bank(j, g), :], op0=ALU.add,
                                               op1=ALU.mult).then_inc(bank_free[bank(j, g)], 1)

            def recur(n, p, link, between=None):
                s = p % 2
                dve.wait_ge(gate_read, n * 24 + (6 * p + 3) + 6)
                link(nc.vector.scalar_tensor_tensor(out=B[:, s, :], in0=B[:, s, :], scalar=1.0, in1=xc[:, p % 2, :],
                                                    op0=ALU.add, op1=ALU.mult))
                dve.wait_ge(th_done, n * 4 + (p + 1))
                nc.vector.scalar_tensor_tensor(out=E[:], in0=E[:], scalar=1.0, in1=R[:],
                                               op0=ALU.add, op1=ALU.mult).then_inc(v_done, 1)
                if between:
                    between()
                dve.wait_ge(root_done, n * 4 + (p + 1))
                nc.vector.scalar_tensor_tensor(out=B[:, s, :], in0=B[:, s, :], scalar=0.5, in1=E[:],
                                               op0=ALU.mult, op1=ALU.mult).then_inc(b_done, 1)
                dve.wait_ge(b_done, n * 4 + (p + 1))
                if p < 2:
                    c, lat, h, end = slice(CTX_COL, CTX_COL + CTX), slice(0, LAT), H0, CTX_COL + CTX - 1
                else:
                    c, lat, h, end = slice(CTX_COL + CTX - 1, CTX_COL - 1, -1), slice(LAT - 1, None, -1), H1, CTX_COL
                    dve.wait_ge(y_stored[s], n * 16)
                link(nc.vector.tensor_tensor_scan(h[:, s, c], A[:, s, c], B[:, s, c], 0.0, ALU.mult, ALU.add))
                nc.vector.tensor_tensor_scan(h[:, s, lat], A[:, s, lat], B[:, s, lat], h[:, s, end:end + 1],
                                             ALU.mult, ALU.add).then_inc(scan_done, 1)

            def combine(n, s, link):
                dve.wait_ge(scan_done, n * 4 + (3 + s))
                link(nc.vector.tensor_tensor(H1[:, s, 0:LAT], H1[:, s, 0:LAT], H0[:, s, 0:LAT], ALU.add))
                nc.vector.scalar_tensor_tensor(out=H1[:, s, 0:LAT], in0=H1[:, s, 0:LAT], scalar=0.5, in1=sg[:, s, :],
                                               op0=ALU.mult, op1=ALU.mult).then_inc(y_done, 1)

            def prologue():
                first = Link(dve, dve_first)
                for q in (slice(0, 1), slice(LAT + 1, CTX_COL + 1), slice(CTX_COL + CTX + 1, QCOLS + 4)):
                    ins = nc.vector.memset(zr[:, q], 0.0)
                first(ins)
                dve.wait_ge(s_const, 80)
                for b in (bra, bri):
                    ins = nc.vector.tensor_scalar(b, b, 0.5, None, ALU.mult)
                first(nc.vector.tensor_scalar(den[:], lam[:], -1.0, None, ALU.mult))
                nc.vector.tensor_tensor(e_[:], den[:], lam[:], ALU.max).then_inc(abs_done, 1)
                nc.vector.tensor_scalar(low[:], lam[:], 0.0, 8.0, ALU.min, ALU.mult)
                dve.wait_ge(e_done, 1)
                first(nc.vector.tensor_scalar(den[:], e_[:], 2.0, None, ALU.add))
                first(nc.vector.reciprocal(den[:], den[:]))
                first(nc.vector.tensor_tensor(z_[:], e_[:], den[:], ALU.mult))
                first(nc.vector.tensor_tensor(z2[:], z_[:], z_[:], ALU.mult))
                first(nc.vector.memset(den[:], 1.0 / (2 * LOG_TERMS - 1)))
                for t in range(LOG_TERMS - 2, -1, -1):
                    first(nc.vector.tensor_tensor(den[:], den[:], z2[:], ALU.mult))
                    first(nc.vector.tensor_scalar(den[:], den[:], 1.0 / (2 * t + 1), None, ALU.add))
                first(nc.vector.scalar_tensor_tensor(out=den[:], in0=den[:], scalar=-16.0, in1=z_[:],
                                                     op0=ALU.mult, op1=ALU.mult))
                first(nc.vector.tensor_tensor(L, den[:], low[:], ALU.add))
                nc.vector.tensor_scalar(Lh, L, 0.5, None, ALU.mult)
                nc.vector.tensor_scalar(nLh, L, -0.5, None, ALU.mult).then_inc(consts_done, 1)
                dve.wait_ge(consts_done, 1)
                conv(-1, 0, 0, first)
                x_low(-1, 0)

            def body(n, last):
                link = Link(dve, dve_link, n, DVE_PER)
                nc.vector.tensor_copy(own[:], lru[:].rearrange("p q (d c) -> p q d c", d=2)[:, :, :, bass.ds(n * 2, 2)]
                                      ).then_inc(own_done, 1)
                conv(n, 1, 2 * n + 1, link)
                silu_z(n, Z0, 0)
                x_low(n, 1)
                silu_z(n, Z0, 1)
                recur(n, 0, link)
                silu_z(n, Z1, 0)
                recur(n, 1, link)
                silu_z(n, Z1, 1)
                recur(n, 2, link)
                combine(n, 0, link)
                if not last:
                    conv(n, 0, 2 * n + 2, link)
                recur(n, 3, link, None if last else lambda: x_low(n, 0))
                combine(n, 1, link)
                assert last or link.n == DVE_PER, link.n

            run(dve, prologue, body)

        @block.tensor
        def _(pe):
            def project(n, j, g):
                slot = (1 + j) % 3
                f, t = GROUPS[g] if j in (X0, X1) else ZGROUPS[g]
                if g == 0:
                    pe.wait_ge(w_lo, chunk(n, j) + 1)
                if not (isinstance(n, int) and half(n, j, g) < 1):
                    pe.wait_ge(bank_free[bank(j, g)], half(n, j, g))
                for c in range(KC):
                    for q, (w, x) in enumerate(((whi, uhi), (whi, ulo), (wlo, uhi))):
                        last = nc.tensor.matmul(ps[:, bank(j, g), 0:t - f], w[:, slot, c * P:(c + 1) * P], x[:, c, f:t],
                                                start=(c == 0 and q == 0), stop=(c == KC - 1 and q == 2))
                last.then_inc(proj, 1)

            def gates(n, p):
                j = GW0 if p < 2 else GW1
                slot = (1 + j) % 3
                if p == 0:
                    pe.wait_ge(xlo_done, 2 * n + 2)
                if p % 2 == 0:
                    pe.wait_ge(w_lo, chunk(n, j) + 1)
                for mat in range(2):
                    for g, (q0, q1) in enumerate(QGROUPS):
                        v = 6 * p + 3 * mat + g
                        pe.wait_ge(gate_read, n * 24 + (v + 1))
                        for c in range(2):
                            at = ((1 - mat) * 2 + c) * 256 + (p % 2) * P
                            for q, (w, x) in enumerate(((whi, xhi), (whi, xlo), (wlo, xhi))):
                                last = nc.tensor.matmul(ps[:, 2 + 3 * mat + g, 0:q1 - q0], w[:, slot, at:at + P],
                                                        x[:, c, q0:q1], start=(c == 0 and q == 0), stop=(c == 1 and q == 2))
                        last.then_inc(gate_mm, 1)

            def prologue():
                for g in range(NG):
                    project(-1, X0, g)

            def body(n, last):
                for g in range(NG):
                    project(n, X1, g)
                project(n, Z0, 0)
                project(n, Z0, 1)
                gates(n, 0)
                project(n, Z1, 0)
                gates(n, 1)
                project(n, Z1, 1)
                gates(n, 2)
                if not last:
                    project(n, X0, 0)
                    project(n, X0, 1)
                    project(n, X0, 2)
                gates(n, 3)

            run(pe, prologue, body)


def columns(v, streams=1):
    v = np.ascontiguousarray(v.reshape(-1, P).T)
    return np.ascontiguousarray(np.repeat(v[:, :, None], streams, axis=2)) if streams > 1 else v


def chunks(w):
    kk, n = w.shape
    return np.ascontiguousarray(w.reshape(kk // P, P, n // P, P).transpose(2, 1, 0, 3)).reshape(n // P, P, kk)


def even_stream():
    B, C, X, G, Q, K, V, BG = (list(range(8 * j, 8 * j + 8)) for j in range(8))
    order = [Q[0], K[0], V[0]]
    for i in range(PAIRS):
        order += [BG[i], C[i], X[i], B[i], G[i]]
        if i + 1 < PAIRS:
            order += [Q[i + 1], K[i + 1], V[i + 1]]
    return order


def out_pieces(w):
    return np.ascontiguousarray(w.reshape(8, 2, P, 2, 512).transpose(3, 0, 2, 1, 4)).reshape(2, 8, P, 1024)


def odd_stream(w_in, w_ra, w_ri):
    c = chunks(w_in)
    g = np.stack([w_ra, w_ri])
    g = g.reshape(2, 2, BLOCKS, 2, P, 256).transpose(2, 1, 4, 0, 3, 5).reshape(BLOCKS, 2, P, 1024)
    rows = [c[0]]
    for n in range(BLOCKS):
        rows += [c[2 * n + 1], c[16 + 2 * n], g[n, 0], c[17 + 2 * n], g[n, 1]]
        if n + 1 < BLOCKS:
            rows.append(c[2 * n + 2])
    return np.ascontiguousarray(np.stack(rows))


def shape_masks():
    cols = np.arange(GRID_W)
    start = np.clip(cols - WIN_C // 2, 0, GRID_W - WIN_C)
    seen = (cols[None, :] >= start[:, None]) & (cols[None, :] < start[:, None] + WIN_C)
    colmask = np.tile(np.where(seen, 0.0, NEG)[::-1], (2, 1)).astype(np.float32)
    rowmask = np.zeros((P, MIDROWS), np.float32)
    rowmask[GRID_W:, MIDROWS - 1] = NEG
    rowmask[:GRID_W, 0] = NEG
    return colmask, rowmask


def layout(x, c, ctx, c_ctx, norm_g, w_ada, b_ada, w_in_e, conv_a, rpb, w_out_e, w_in_o, conv_c, conv_c_b,
           w_ra, b_ra, w_ri, b_ri, lru_lam, w_out_o, final_g):
    n = {key: np.asarray(v) for key, v in locals().items()}
    colmask, rowmask = shape_masks()
    bias_rows = np.zeros((16, TROWS + 1, P), np.float32)
    bias_rows[:, 1:TROWS, GRID_W - WIN_C:GRID_W + WIN_C - 1] = n["rpb"][0]
    ada = n["w_ada"]
    b_cols = columns(n["b_ada"].reshape(-1), 2)
    arrays = dict(
        x=n["x"], ctx=n["ctx"],
        ident=np.eye(P, dtype=np.float32),
        c_cols=np.ascontiguousarray(np.stack([columns(n["c"][0]), columns(n["c_ctx"])], axis=2)),
        bada=b_cols,
        normg=np.ascontiguousarray(columns(n["norm_g"].reshape(-1), 2).reshape(P, 2, KC, 2)),
        w_ada=np.ascontiguousarray(ada.reshape(2, 2, 4, P, 6, 512).transpose(0, 4, 1, 3, 2, 5)).reshape(12, 2, P, 2048),
        w_even=chunks(n["w_in_e"][0])[even_stream()],
        conv_a=np.ascontiguousarray(n["conv_a"][0].reshape(3, 8, P).transpose(2, 1, 0)).reshape(P, 24),
        bias_rows=bias_rows, colmask=colmask, rowmask=rowmask,
        w_out0=out_pieces(n["w_out_e"][0]), w_out1=out_pieces(n["w_out_o"][0]),
        w_odd=odd_stream(n["w_in_o"][0], n["w_ra"][0], n["w_ri"][0]),
        conv_c=np.ascontiguousarray(n["conv_c"][0].reshape(4, 16, P).transpose(2, 1, 0)).reshape(P, 64),
        conv_b=columns(n["conv_c_b"][0]),
        b_ra=columns(n["b_ra"].reshape(-1)), b_ri=columns(n["b_ri"].reshape(-1)),
        lam=columns(n["lru_lam"].reshape(-1)),
        final_g=n["final_g"],
    )
    return {key: np.ascontiguousarray(v) for key, v in arrays.items()}


def kernel(**inputs):
    import concourse.bacc as bacc
    from concourse.bass_utils import run_bass_kernel_spmd

    nc = bacc.Bacc("TRN2", target_bir_lowering=False, num_devices=1)
    arrays = layout(**inputs)
    aps = {name: nc.dram_tensor(f"in_{name}", v.shape, mybir.dt.from_np(v.dtype), kind="ExternalInput").ap()
           for name, v in arrays.items()}
    out = nc.dram_tensor("out", (1, LAT, D), F32, kind="ExternalOutput").ap()
    build_program(nc, aps, out)
    r = run_bass_kernel_spmd(nc, [{f"in_{name}": v for name, v in arrays.items()}], core_ids=[0])
    return r.results[0]["out"]
```
